# Optimizing a Trainium2 kernel written in Bass

```python
import jax, jax.numpy as jnp
from jax import lax
import numpy as np

D_MODEL = 1024
BATCH = 1
SEQ = 1024
DEPTH = 1

CHUNK = 64
N_MEM = 256
EPS = 1e-6
GLA_HEADS = 4
GLA_DK = 64
GLA_DV = 128
GLA_WIDTH = GLA_HEADS * GLA_DV
GLA_KW = GLA_HEADS * GLA_DK
GATE_RANK = 16
GATE_TAU = 16.0
SG_WIDTH = D_MODEL - GLA_WIDTH
SG_GROUPS = 4
SG_GROUP_CH = SG_WIDTH // SG_GROUPS
SG_BLOCK = 128
X_HEADS = 4
X_HEAD_DIM = D_MODEL // X_HEADS
D_FF = -(-8 * D_MODEL // (3 * 256)) * 256
OFF_Q = 0
OFF_K = OFF_Q + GLA_KW
OFF_V = OFF_K + GLA_KW
OFF_G = OFF_V + GLA_WIDTH
OFF_A = OFF_G + GLA_WIDTH
OFF_U = OFF_A + GATE_RANK
OFF_SV = OFF_U + SG_WIDTH
D_IN = OFF_SV + SG_WIDTH

kernel_name = "hybrid_gla_gmlp_memxattn_sandwich"

def rmsnorm(x, g):
    xf = x.astype(jnp.float32)
    y = xf * lax.rsqrt(jnp.mean(xf * xf, axis=-1, keepdims=True) + EPS)
    return (y * g.astype(jnp.float32)).astype(x.dtype)

def layernorm(x, g, b):
    xf = x.astype(jnp.float32)
    mu = jnp.mean(xf, axis=-1, keepdims=True)
    var = jnp.mean(jnp.square(xf - mu), axis=-1, keepdims=True)
    y = (xf - mu) * lax.rsqrt(var + EPS)
    return (y * g.astype(jnp.float32) + b.astype(jnp.float32)).astype(x.dtype)

def gla_mixer(q, k, v, g, a_lr, w_gate_up, b_gate, onorm):
    B, S, _ = q.shape
    nc = S // CHUNK
    qc = q.reshape(B, nc, CHUNK, GLA_HEADS, GLA_DK).astype(jnp.float32) * (GLA_DK ** -0.5)
    kc = k.reshape(B, nc, CHUNK, GLA_HEADS, GLA_DK).astype(jnp.float32)
    vc = v.reshape(B, nc, CHUNK, GLA_HEADS, GLA_DV).astype(jnp.float32)
    loga = jax.nn.log_sigmoid((a_lr @ w_gate_up + b_gate).astype(jnp.float32)) / GATE_TAU
    loga = loga.reshape(B, nc, CHUNK, GLA_HEADS, GLA_DK)
    cum = jnp.cumsum(loga, axis=2)
    cum_end = cum[:, :, -1:]
    k_dec = kc * jnp.exp(cum_end - cum)
    u_c = jnp.einsum('bnchk,bnchv->nbhkv', k_dec, vc)
    a_c = jnp.moveaxis(jnp.exp(cum_end[:, :, 0]), 1, 0)

    def step(state, inp):
        a, u = inp
        state = a[..., None] * state + u
        return state, state

    s0 = jnp.zeros((B, GLA_HEADS, GLA_DK, GLA_DV), jnp.float32)
    _, states = lax.scan(step, s0, (a_c, u_c))
    o = jnp.einsum('bnchk,nbhkv->bnchv', qc, states).reshape(B, S, GLA_HEADS, GLA_DV)
    o = o * lax.rsqrt(jnp.mean(o * o, axis=-1, keepdims=True) + EPS)
    o = o.reshape(B, S, GLA_WIDTH) * onorm.astype(jnp.float32)
    return (o * jax.nn.silu(g.astype(jnp.float32))).astype(q.dtype)

def spatial_gating_mixer(u, sv, ln_g, ln_b, w_s, b_s):
    B, S, _ = u.shape
    nb = S // SG_BLOCK
    u = jax.nn.gelu(u)
    sv = layernorm(jax.nn.gelu(sv), ln_g, ln_b)
    pos = jnp.arange(SG_BLOCK) // CHUNK
    mask = (pos[None, :] <= pos[:, None]).astype(w_s.dtype)
    svb = sv.reshape(B, nb, SG_BLOCK, SG_GROUPS, SG_GROUP_CH)
    z = jnp.einsum('gij,bnjgc->bnigc', w_s * mask, svb) + b_s.T[None, None, :, :, None]
    return u * z.reshape(B, S, SG_WIDTH)

def memory_cross_attention(xn, memn, w_xq, w_xkv, w_xo):
    B, S, _ = xn.shape
    q = (xn @ w_xq).reshape(B, S, X_HEADS, X_HEAD_DIM)
    kv = memn @ w_xkv
    k = kv[..., :D_MODEL].reshape(B, N_MEM, X_HEADS, X_HEAD_DIM)
    v = kv[..., D_MODEL:].reshape(B, N_MEM, X_HEADS, X_HEAD_DIM)
    s = jnp.einsum('bshd,bmhd->bhsm', q, k).astype(jnp.float32) * (X_HEAD_DIM ** -0.5)
    p = jax.nn.softmax(s, axis=-1).astype(v.dtype)
    o = jnp.einsum('bhsm,bmhd->bshd', p, v).reshape(B, S, D_MODEL)
    return o @ w_xo

def swiglu_ffn(xn, w_gu, w_down):
    h = xn @ w_gu
    return (jax.nn.silu(h[..., :D_FF]) * h[..., D_FF:]) @ w_down

def setup_inputs(seed: int = 0) -> dict:
    key = jax.random.key(seed)
    ks = jax.random.split(key, 24)
    L = DEPTH

    def w(k, shape, fan_in):
        return jax.random.normal(k, shape, jnp.float32) * (fan_in ** -0.5)

    def gain(k, shape):
        return 1.0 + 0.02 * jax.random.normal(k, shape, jnp.float32)

    def small(k, shape):
        return 0.02 * jax.random.normal(k, shape, jnp.float32)

    return {
        "x": jax.random.normal(ks[0], (BATCH, SEQ, D_MODEL), jnp.float32),
        "mem": jax.random.normal(ks[1], (BATCH, N_MEM, D_MODEL), jnp.float32),
        "norm_mix_pre": gain(ks[2], (L, D_MODEL)),
        "w_in": w(ks[3], (L, D_MODEL, D_IN), D_MODEL),
        "w_gate_up": w(ks[4], (L, GATE_RANK, GLA_KW), GATE_RANK),
        "b_gate": 0.5 + 0.1 * jax.random.normal(ks[5], (L, GLA_KW), jnp.float32),
        "gla_onorm": gain(ks[6], (L, GLA_WIDTH)),
        "sg_ln_g": gain(ks[7], (L, SG_WIDTH)),
        "sg_ln_b": small(ks[8], (L, SG_WIDTH)),
        "w_spatial": 0.5 * w(ks[9], (L, SG_GROUPS, SG_BLOCK, SG_BLOCK), SG_BLOCK),
        "b_spatial": gain(ks[10], (L, SG_GROUPS, SG_BLOCK)),
        "w_out": w(ks[11], (L, GLA_WIDTH + SG_WIDTH, D_MODEL), GLA_WIDTH + SG_WIDTH),
        "norm_mix_post": gain(ks[12], (L, D_MODEL)),
        "norm_x_pre": gain(ks[13], (L, D_MODEL)),
        "norm_mem": gain(ks[14], (L, D_MODEL)),
        "w_xq": w(ks[15], (L, D_MODEL, D_MODEL), D_MODEL),
        "w_xkv": w(ks[16], (L, D_MODEL, 2 * D_MODEL), D_MODEL),
        "w_xo": w(ks[17], (L, D_MODEL, D_MODEL), D_MODEL),
        "norm_x_post": gain(ks[18], (L, D_MODEL)),
        "norm_ffn_pre": gain(ks[19], (L, D_MODEL)),
        "w_ffn_gu": w(ks[20], (L, D_MODEL, 2 * D_FF), D_MODEL),
        "w_ffn_down": w(ks[21], (L, D_FF, D_MODEL), D_FF),
        "norm_ffn_post": gain(ks[22], (L, D_MODEL)),
    }

def reference(x, mem, norm_mix_pre, w_in, w_gate_up, b_gate, gla_onorm, sg_ln_g, sg_ln_b,
              w_spatial, b_spatial, w_out, norm_mix_post, norm_x_pre, norm_mem, w_xq, w_xkv,
              w_xo, norm_x_post, norm_ffn_pre, w_ffn_gu, w_ffn_down, norm_ffn_post):
    for l in range(DEPTH):
        xn = rmsnorm(x, norm_mix_pre[l])
        h = xn @ w_in[l]
        gla_out = gla_mixer(h[..., OFF_Q:OFF_K], h[..., OFF_K:OFF_V], h[..., OFF_V:OFF_G],
                            h[..., OFF_G:OFF_A], h[..., OFF_A:OFF_U],
                            w_gate_up[l], b_gate[l], gla_onorm[l])
        sg_out = spatial_gating_mixer(h[..., OFF_U:OFF_SV], h[..., OFF_SV:D_IN],
                                      sg_ln_g[l], sg_ln_b[l], w_spatial[l], b_spatial[l])
        mix = jnp.concatenate([gla_out, sg_out], axis=-1) @ w_out[l]
        x = x + rmsnorm(mix, norm_mix_post[l])
        xa = memory_cross_attention(rmsnorm(x, norm_x_pre[l]), rmsnorm(mem, norm_mem[l]),
                                    w_xq[l], w_xkv[l], w_xo[l])
        x = x + rmsnorm(xa, norm_x_post[l])
        f = swiglu_ffn(rmsnorm(x, norm_ffn_pre[l]), w_ffn_gu[l], w_ffn_down[l])
        x = x + rmsnorm(f, norm_ffn_post[l])
    return x


_drawn_inputs = setup_inputs


def setup_inputs(seed=0):
    import zlib

    import numpy as np

    out = dict(_drawn_inputs(seed))
    spreads = {}
    factors = {'gla_onorm': 5.458,
     'sg_ln_g': 8.0,
     'sg_ln_b': 8.0,
     'b_spatial': 5.197,
     'norm_mix_post': 3.613,
     'norm_x_pre': 4.205,
     'norm_mem': 2.992,
     'norm_x_post': 13.821,
     'norm_ffn_pre': 11.247,
     'norm_ffn_post': 22.961}
    for name, (base, spread) in spreads.items():
        noise = np.random.default_rng([zlib.crc32(name.encode()), seed]).standard_normal(out[name].shape)
        drawn = base * np.exp(spread * noise) if base else spread * noise
        out[name] = __import__('jax').numpy.asarray(drawn.astype(out[name].dtype))
    for name, factor in factors.items():
        out[name] = (out[name] * factor).astype(out[name].dtype)
    return out
```

```python
from contextlib import ExitStack

import concourse.bass as bass
from concourse import mybir

F32 = mybir.dt.float32
F32R = mybir.dt.float32r
ACT = mybir.ActivationFunctionType
ALU = mybir.AluOpType
AX = mybir.AxisListType

P = 128
EPS = 1e-6
CHUNK = 64
HEADS = 4
DK, DV = 64, 128
RANK = 16
GATE_TAU = 16.0
MM_BANKS = 3
LAG = 3


def build(nc, x, mem, norm_mix_pre, w_in, w_gate_up, b_gate, gla_onorm, sg_ln_g, sg_ln_b,
          w_spatial, b_spatial, w_out, norm_mix_post, norm_x_pre, norm_mem, w_xq, w_xkv,
          w_xo, norm_x_post, norm_ffn_pre, w_ffn_gu, w_ffn_down, norm_ffn_post, out):
    _, T, D = x.shape
    NM = mem.shape[1]
    KT, TT, MT = D // P, T // P, NM // P
    CW = 512
    GW = HEADS * DV
    KW = HEADS * DK
    DFF = w_ffn_down.shape[1]
    FT = DFF // P
    OFF_V = 2 * KW
    OFF_G = OFF_V + GW
    OFF_A = OFF_G + GW
    OFF_U = OFF_A + RANK
    OFF_SV = OFF_U + (D - GW)
    XD = D // HEADS
    assert T == 1024 and D == 1024 and NM == 256 and XD == 256 and FT == 22

    w_in, w_xq, w_xkv, w_xo, w_out = w_in[0], w_xq[0], w_xkv[0], w_xo[0], w_out[0]
    w_gu, w_down = w_ffn_gu[0], w_ffn_down[0]
    s_dram = nc.dram_tensor("score_weights", [D, HEADS * NM], F32, kind="Internal").ap()
    o_dram = nc.dram_tensor("output_weights", [HEADS * NM, D], F32, kind="Internal").ap()

    CHUNKS = [("xk", 0), ("xq", 0), ("xk", 1), ("xq", 1), ("xv", 0), ("xv", 1), ("xo", 0), ("xo", 1),
              ("qk", 0), ("v", 0), ("g", 0), ("sv", 0), ("u", 0), ("wo", 0), ("wo", 1),
              ("s", 0), ("s", 1), ("o", 0), ("o", 1)]
    CNO = {c: n for n, c in enumerate(CHUNKS)}
    SRC = {"xk": (w_xkv, 0), "xv": (w_xkv, D), "xq": (w_xq, 0), "xo": (w_xo, 0), "qk": (w_in, 0),
           "v": (w_in, OFF_V), "g": (w_in, OFF_G), "sv": (w_in, OFF_SV), "u": (w_in, OFF_U),
           "wo": (w_out, 0), "s": (s_dram, 0), "o": (o_dram, 0)}
    NPIECE = 4 * len(CHUNKS)
    NRAW = 3

    def is_split(p):
        return CHUNKS[p // 4][0] != "xq"

    def splits(p):
        return sum(is_split(q) for q in range(p + 1))

    NSPLIT = splits(NPIECE - 1)

    def gu_piece(i, half):
        return NPIECE + half if isinstance(i, int) and i == 0 else i * 3 + (NPIECE - 1 + half)

    def dn_piece(i):
        return i * 3 + (NPIECE + 4 - (2 if isinstance(i, int) and i == FT - 1 else 0))

    def ffn_splits(piece):
        return piece + (1 - NPIECE + NSPLIT)

    STEPS = []
    for name, b in CHUNKS:
        if name in ("xk", "xv"):
            STEPS += [(name, b, f) for f in range(4)]
        elif name == "qk":
            STEPS += [("q", 0, f) for f in range(4)] + [("a", 0, f) for f in range(2)]
            STEPS += [("k", 0, t) for t in range(TT)]
        else:
            STEPS += [(name, b, t) for t in range(TT)]
    SNO = {s: n for n, s in enumerate(STEPS)}

    def chunk_of(s):
        return CNO[("qk", 0)] if s[0] in "qak" and s[0] in ("q", "a", "k") else CNO[(s[0], s[1])]

    FIRST = {chunk_of(s): n for n, s in reversed(list(enumerate(STEPS)))}
    LAST = {chunk_of(s): n for n, s in enumerate(STEPS)}

    def freed_by(s):
        return "dve" if s[0] in ("xk", "xv", "q", "a", "wo", "o") else "act"

    def free_count(n, who):
        return sum(freed_by(s) == who for s in STEPS[:n + 1])

    TR_AT = {n: [] for n in range(len(STEPS) + LAG)}
    TR_AT[SNO["xk", 0, 0]] += [("mem", 0), ("mem", 1)]
    for b in range(2):
        for j, s in enumerate([("xk", b, 1), ("xk", b, 3), ("xq", b, 0), ("xq", b, 2)]):
            TR_AT[SNO[s]].append(("xq", 4 * b + j))
    for t in range(TT):
        TR_AT[SNO["u", 0, t] + LAG].append(("mix", t))
        TR_AT[SNO["wo", 1, t] + LAG].append(("xn2", t))
        TR_AT[SNO["s", 1, t] + LAG].append(("probs", t))
        TR_AT[SNO["o", 1, t] + LAG].append(("xn3", t))
    TR_AT[SNO["xo", 1, 0]].append(("ws", 0))
    X_TR = [("xk", 1, 0), ("xk", 1, 2), ("xq", 1, 0), ("xq", 1, 4), ("xv", 0, 1), ("xv", 0, 3), ("xv", 1, 1), ("xv", 1, 3)]
    X_NORM = {SNO[s] - 1: t for t, s in enumerate(X_TR)}
    X_BEFORE = dict(zip((8, 9, 15, 16, 18, 21, 25, 27), range(TT)))
    for t, s in enumerate(X_TR):
        TR_AT[SNO[s]].append(("x", t))
    TRS = [g for n in sorted(TR_AT) for g in TR_AT[n]]
    TRNO = {g: n for n, g in enumerate(TRS)}

    SPLIT_AT = {n: [] for n in range(-1, len(STEPS))}
    SPLIT_AT[-1] = [0, 1, 2, 3]
    for c, (name, b) in enumerate(CHUNKS):
        if name == "xq" or c == 0:
            continue
        at = {("xk", 1): [("xq", 0, j) for j in (3, 4, 5, 6)],
              ("xv", 0): [("xq", 1, j) for j in (3, 4, 5, 6)]}.get((name, b))
        if at is None:
            f, n = FIRST[c - 1], LAST[c - 1] - FIRST[c - 1] + 1
            at = [STEPS[f + (j * n) // 4] for j in range(4)]
        for j, s in enumerate(at):
            SPLIT_AT[SNO[s]].append(4 * c + j)
    for j in range(4):
        SPLIT_AT[SNO["o", 1, 2 * j]].append(NPIECE + j)

    JOBS = [("mem", 0), ("mem", 1)] + [("x", t) for t in range(TT)]
    JOBS += [("gla", t) for t in range(TT)] + [("ln", t) for t in range(TT)]
    for st in ("wo", "o"):
        for t in range(TT):
            JOBS += [(st + "_y", t), (st + "_x", t)]
    JOBS += [("ffn_y", t) for t in range(TT)]
    JNO = {j: n for n, j in enumerate(JOBS)}

    def squares(job):
        return sum(j[0] != "ln" for j in JOBS[:JNO[job] + 1])

    XHS = [("mem", 0), ("mem", 1)] + [(n, t) for n in ("x", "xn2", "xn3") for t in range(TT)]
    XHNO = {g: n for n, g in enumerate(XHS)}

    ctx = ExitStack()
    with ctx:
        base = (nc.sbuf_base + 63) // 64 * 64
        K = 1024
        at = {}
        pos = base
        for name, size in (("act_hi", 32 * K), ("act_lo", 32 * K), ("w_hi", 32 * K), ("w_lo", 32 * K),
                           ("raw", 12 * K), ("resid", 32 * K), ("half", 16 * K), ("tok", 8 * K),
                           ("gain", 4 * K), ("spare", 2 * K), ("small", 0)):
            at[name] = pos
            pos += size
        small = [at["small"]]

        def place(name, shape, dt, offset):
            return nc.alloc_sbuf_tensor_at(name, shape, dt, offset=offset)

        def little(name, shape, dt=F32):
            size = 4
            for s in shape[1:]:
                size *= s
            o = small[0]
            small[0] += (size + 31) // 32 * 32
            assert small[0] <= nc.sbuf_usable_end, small[0] - nc.sbuf_usable_end
            return place(name, shape, dt, o)

        act_hi = place("act_hi", [P, KT, T], F32R, at["act_hi"])
        act_lo = place("act_lo", [P, KT, T], F32R, at["act_lo"])
        w_hi = place("w_hi", [P, 2, KT, CW], F32R, at["w_hi"])
        w_lo = place("w_lo", [P, 2, KT, CW], F32R, at["w_lo"])
        raw = place("raw", [P, NRAW, 2 * CW], F32, at["raw"])
        resid = place("resid", [P, TT, D], F32, at["resid"])
        kv_hi = place("kv_hi", [P, 2 * KT, NM], F32R, at["resid"])
        kv_lo = place("kv_lo", [P, 2 * KT, NM], F32R, at["resid"] + 16 * K)
        half = place("half", [P, TT, CW], F32, at["half"])
        memT_hi = place("memT_hi", [P, KT, NM], F32R, at["half"])
        memT_lo = place("memT_lo", [P, KT, NM], F32R, at["half"] + 8 * K)
        raw_a = place("raw_a", [P, KT, RANK], F32, at["half"])
        raw_ws = place("raw_ws", [P, HEADS, P], F32, at["half"] + 4 * K)
        tok = place("tok", [P, 2, D], F32, at["tok"])
        state = place("state", [P, 2, 2, 2, P], F32, at["tok"])
        aT = place("aT", [P, T], F32, at["tok"] + 4 * K)
        gain = place("gain", [P, D], F32, at["gain"])
        spare = place("spare", [P, CW], F32, at["spare"])
        stage = place("stage", [P, 3, CW], F32, at["gain"])
        wa = place("wa", [P, KT, CHUNK], F32R, at["spare"])
        wsT = little("wsT", [P, HEADS, P])
        hid = [spare, wsT[:, :, :].rearrange("p a b -> p (a b)")]
        ident = little("ident", [P, P])
        later = little("later", [P, P])
        inchunk = little("inchunk", [P, 2])
        wg = little("wg", [P, KW])
        decay = little("decay", [P, TT, 4])
        VECTORS = [("mem", norm_mem, KT), ("mix", norm_mix_pre, KT), ("x", norm_x_pre, KT),
                   ("ffn", norm_ffn_pre, KT), ("gla", gla_onorm, HEADS), ("bsp", b_spatial, HEADS)]
        NVEC = sum(v[2] for v in VECTORS)
        columns = little("columns", [P, NVEC])
        vec_rows = wsT[0:NVEC, 0, :]
        pre, o = {}, 0
        for name, _, w in VECTORS:
            pre[name] = columns[:, o:o + w]
            o += w
        bsp = pre["bsp"]
        mhalf = little("mhalf", [P, 4])
        ss = little("ss", [P, 2, 4])
        ssh = little("ssh", [P, TT])
        var = little("var", [P, 4])
        rstd = little("rstd", [P, 4, 4])
        bn = little("bn", [P, 6])
        mv = little("mv", [P, 2, 2])
        top = little("top", [P, 2, 2])
        den = little("den", [P, 2, 2])
        wf_hi = w_hi[:, :, :, :].rearrange("p s k n -> p (s k n)")
        wf_lo = w_lo[:, :, :, :].rearrange("p s k n -> p (s k n)")
        HALF_W = KT * CW

        def gu(w, i2):
            return w[:, HALF_W + i2 * KT * 2 * P:HALF_W + (i2 + 1) * KT * 2 * P].rearrange(
                "p (k g n) -> p k g n", k=KT, g=2)

        def hidden(w, i2):
            return w[:, i2 * T:(i2 + 1) * T]

        def dn(w, last=False):
            o = HALF_W if last else 2 * T
            return w[:, o:o + D]

        acc67 = [place("acc6", [P, D], F32, at["w_hi"] + 12 * K), place("acc7", [P, D], F32, at["w_lo"] + 12 * K)]
        halfd = half[:, :, :].rearrange("p (a b) n -> p a (b n)", b=2)
        acc = [halfd[:, t, :] for t in range(4)] + [tok[:, 0, :], tok[:, 1, :], acc67[0][:, :], acc67[1][:, :]]

        ps = ctx.enter_context(nc.psum_tensor("ps", [P, 8, CW], F32))
        Z, TR, U, O = 3, 4, 6, 7
        SUF = TR

        def kv_psum(rows, c, pr):
            return ps[rows, (U, TR + 1)[c], pr * P:(pr + 1) * P]

        def o_psum(rows, h):
            return ps[rows, (O, TR)[h % 2], (h // 2) * DV:(h // 2 + 1) * DV]

        def sg_psum(t, h):
            return ps[:, (U, O)[t % 2], h * P:(h + 1) * P]

        def sem(name):
            return ctx.enter_context(nc.semaphore(name))

        raw_landed = [sem(f"raw_landed{i}") for i in range(NRAW)]
        gu0_landed, gu_landed = [[sem(f"{n}_landed{h}") for h in range(2)] for n in ("gu0", "gu")]
        dn_landed = sem("dn_landed")
        mem_landed, small_landed = sem("mem_landed"), sem("small_landed")
        rows_landed, rows_turned, columns_ready = sem("rows_landed"), sem("rows_turned"), sem("columns_ready")
        x_landed = [sem(f"x_landed{i}") for i in range(2)]
        x_back = [sem(f"x_back{i}") for i in range(TT)]
        part_landed, gains_landed = sem("part_landed"), sem("gains_landed")
        stored, out_stored = [sem(f"stored{i}") for i in range(3)], sem("out_stored")
        consts = sem("consts")
        hi_split, lo_split = sem("hi_split"), sem("lo_split")
        squared, rstd_ready, xh_ready = sem("squared"), sem("rstd_ready"), sem("xh_ready")
        tr_done, tr_hi, tr_lo = sem("tr_done"), sem("tr_hi"), sem("tr_lo")
        mm_done, free_act, free_dve = sem("mm_done"), sem("free_act"), sem("free_dve")
        kv_hi_done = sem("kv_hi_done")
        wa_ready, aT_ready = sem("wa_ready"), sem("aT_ready")
        z_done, z_read, gate_e, gate_l, loga_ready = (sem("z_done"), sem("z_read"), sem("gate_e"),
                                                      sem("gate_l"), sem("loga_ready"))
        suf_done, suf_read, kdec_ready = sem("suf_done"), sem("suf_read"), sem("kdec_ready")
        u_done, state_ready, o_done, gla_ready = (sem("u_done"), sem("state_ready"), sem("o_done"),
                                                  sem("gla_ready"))
        silu_ready = sem("silu_ready")
        svg_ready, bn_ready, ln_ready = sem("svg_ready"), sem("bn_ready"), sem("ln_ready")
        sg_done, ug_ready, mix_ready = sem("sg_done"), sem("ug_ready"), sem("mix_ready")
        y_squared, resid_ready = sem("y_squared"), sem("resid_ready")
        top_ready, exp_ready, probs_ready = sem("top_ready"), sem("exp_ready"), sem("probs_ready")
        gu_done, silu_done, prod_done, hid_hi, hid_lo = (sem("gu_done"), sem("silu_done"), sem("prod_done"),
                                                         sem("hid_hi"), sem("hid_lo"))
        dn_done, added = sem("dn_done"), sem("added")
        gained, final_ready = sem("gained"), sem("final_ready")
        act_own, dve_own, pool_own = sem("act_own"), sem("dve_own"), sem("pool_own")

        def y_first(kind, t):
            return t + 1 + (TT if kind == "o" else 0)

        def wait_free(eng, n):
            if n >= MM_BANKS:
                who = freed_by(STEPS[n - MM_BANKS])
                eng.wait_ge(free_act if who == "act" else free_dve, free_count(n - MM_BANKS, who))

        def bank(n, w=CW):
            return ps[:, n % MM_BANKS, 0:w]

        def tr_source(g):
            kind, i = g
            if kind == "xq":
                v = raw[:, (4 * (1 + 2 * (i // 4)) + i % 4) % NRAW, :].rearrange("p (k f n) -> p f k n", k=2, f=4)
                return [v[:, f, k, :] for f in range(4) for k in range(2)]
            if kind == "mix":
                v = resid[:, i, :]
            elif kind == "ws":
                return [raw_ws[:, h, :] for h in range(HEADS)]
            elif kind == "probs":
                return [half[:, i, h * P:(h + 1) * P] for h in range(4)] + \
                       [tok[:, i % 2, h * P:(h + 1) * P] for h in range(4)]
            else:
                v = tok[:, i % 2, :]
            return [v[:, k * P:(k + 1) * P] for k in range(KT)]

        def tr_target(g, b, hi):
            kind, i = g
            if kind == "mem":
                w = memT_hi if hi else memT_lo
                return w[:, 4 * b:4 * b + 4, i * P:(i + 1) * P]
            if kind == "xq":
                w = (w_hi if hi else w_lo)[:, 1, :, :].rearrange("p k n -> p (k n)").rearrange(
                    "p (f d) -> p f d", f=4)
                return w[:, 2 * b:2 * b + 2, (i % 4) * 2 * P:(i % 4 + 1) * 2 * P]
            w = act_hi if hi else act_lo
            return w[:, 4 * b:4 * b + 4, i * P:(i + 1) * P]

        def tr_bank(g, b):
            n = 2 if g[0] == "xq" else 4
            return ps[:, TR + b, :].rearrange("p (a n) -> p a n", a=n)

        def piece_gain(p):
            if p >= NPIECE:
                return pre["ffn"]
            name, _ = CHUNKS[p // 4]
            if name in ("xk", "xv"):
                return pre["mem"]
            if name in ("qk", "v", "g", "sv", "u"):
                return pre["mix"]
            if name == "wo":
                return pre["gla"] if p % 4 < 2 else None
            return pre["x"] if name == "s" else None

        def split_parts(p):
            g = piece_gain(p)
            if p >= NPIECE:
                i, h = (p - NPIECE) // 2, (p - NPIECE) % 2
                return gu_parts(i, h, p % NRAW)
            c, j = divmod(p, 4)
            r = raw[:, p % NRAW, :].rearrange("p (k n) -> p k n", k=2)
            if g is None:
                return [(None, r, lambda w: w[:, c % 2, 2 * j:2 * j + 2, :])]
            return [(g[:, 2 * j + k:2 * j + k + 1], r[:, k, :],
                     (lambda k: lambda w: w[:, c % 2, 2 * j + k, :])(k)) for k in range(2)]

        def gu_parts(i2, h, slot):
            r = raw[:, slot, :].rearrange("p (k n) -> p k n", k=4)
            def at_(k):
                return lambda w: gu(wf_hi if w is w_hi else wf_lo, i2 % 2)[:, 4 * h + k, :, :].rearrange(
                    "p g n -> p (g n)")
            return [(pre["ffn"][:, 4 * h + k:4 * h + k + 1], r[:, k, :], at_(k)) for k in range(4)]

        def splits_hi(eng, parts):
            for g, r, dst in parts:
                if g is None:
                    last = nc.scalar.activation(dst(w_hi), r, ACT.Copy)
                else:
                    last = nc.scalar.activation(dst(w_hi), r, ACT.Copy, scale=g)
            last.then_inc(hi_split, 1)

        def splits_lo(eng, parts):
            for g, r, dst in parts:
                h = dst(w_hi).bitcast(F32)
                if g is None:
                    last = nc.vector.tensor_tensor(dst(w_lo), r, h, ALU.subtract)
                else:
                    last = nc.vector.scalar_tensor_tensor(out=dst(w_lo), in0=r, scalar=g, in1=h,
                                                          op0=ALU.mult, op1=ALU.subtract)
            last.then_inc(lo_split, 1)

        def landed(eng, p):
            if p < NPIECE:
                eng.wait_ge(raw_landed[p % NRAW], 16 * (p // NRAW + 1))
            else:
                i, h = divmod(p - NPIECE, 2)
                eng.wait_ge((gu_landed if i else gu0_landed)[h], 32)

        def slot_free(eng, p):
            if p >= NPIECE:
                eng.wait_ge(mm_done, LAST[CNO[("o", 0)]] + 1)
            elif p // 4 >= 2:
                eng.wait_ge(mm_done, LAST[p // 4 - 2] + 1)

        block = ctx.enter_context(nc.Block())

        @block.sync
        def _(sp):
            memd = mem[0].rearrange("(t p) d -> p t d", p=P)
            xd = x[0].rearrange("(t p) d -> t p d", p=P)

            def piece(p):
                if p >= NRAW:
                    q = p - NRAW
                    if q < NPIECE and not is_split(q):
                        c, j = divmod(q, 4)
                        sp.wait_ge(tr_done, TRNO["xq", 4 * (c // 2) + j] + 1)
                    elif q < NPIECE:
                        sp.wait_ge(lo_split, splits(q))
                    else:
                        sp.wait_ge(lo_split, ffn_splits(q))
                if p >= NPIECE:
                    i, h = (p - NPIECE) // 2, (p - NPIECE) % 2
                    gu_dma(i, h, p % NRAW, (gu0_landed if i == 0 else gu_landed)[h])
                    return
                (name, b), j = CHUNKS[p // 4], p % 4
                w, off = SRC[name]
                if name in ("s", "o") and j == 0 and b == 0:
                    for s in range(3):
                        n = sum((k % 3) == s for k in range(16 if name == "s" else 32))
                        sp.wait_ge(stored[s], 16 * n)
                src = w[2 * j * P:(2 * j + 2) * P, off + b * CW:off + (b + 1) * CW]
                sp.dma_start(raw[:, p % NRAW, :].rearrange("p (k n) -> p k n", k=2),
                             src.rearrange("(k p) n -> p k n", p=P)).then_inc(raw_landed[p % NRAW], 16)

            def gu_dma(i, h, slot, landed_):
                dst = raw[:, slot, :].rearrange("p (k g n) -> p k g n", k=4, g=2)
                rows = w_gu[h * 4 * P:(h + 1) * 4 * P, :].rearrange("(k p) (g n) -> p k g n", p=P, g=2)
                for g in range(2):
                    sp.dma_start(dst[:, :, g, :], rows[:, :, g, bass.ds(i * P, P)]).then_inc(landed_, 16)

            def x_in(t):
                sp.wait_ge(tr_done, TRNO[("mem", t) if t < 2 else ("x", t - 2)] + 1)
                sp.dma_start(tok[:, t % 2, :], xd[t]).then_inc(x_landed[t % 2], 16)

            sp.dma_start(tok[:, :, :], memd).then_inc(mem_landed, 16)
            for p in range(NPIECE + 4):
                if p in X_BEFORE:
                    x_in(X_BEFORE[p])
                piece(p)
                if p == 29:
                    sp.wait_ge(mm_done, SNO["xv", 1, 3] + 1)
                    sp.dma_start(raw_a[:, :, :], w_in[:, OFF_A:OFF_A + RANK].rearrange(
                        "(k p) n -> p k n", p=P)).then_inc(part_landed, 16)
                    sp.dma_start(raw_ws[:, :, :], w_spatial[0].rearrange("g i j -> i g j")).then_inc(part_landed, 16)
                if p == 4 * CNO[("g", 0)] + 3:
                    for s in range(3):
                        sp.wait_ge(stored[s], 16 * sum((k % 3) == s for k in range(32)))
                    sp.dma_start(gain[:, 0:GW], sg_ln_g[0:1, :].broadcast_to([P, GW])).then_inc(gains_landed, 16)
                    sp.dma_start(gain[:, GW:D], sg_ln_b[0:1, :].broadcast_to([P, GW])).then_inc(gains_landed, 16)
                if p == 4 * CNO[("wo", 0)] + 3:
                    sp.wait_ge(ln_ready, TT)
                    sp.dma_start(gain[:, :], norm_mix_post[0:1, :].broadcast_to([P, D])).then_inc(gains_landed, 16)
                c, j = divmod(p, 4)
                if c in (CNO[("wo", 1)], CNO[("s", 0)]):
                    for t in ((2 * j - 2, 2 * j - 1) if c == CNO[("wo", 1)] else (2 * j + 6, 2 * j + 7)):
                        if 0 <= t < TT:
                            sp.wait_ge(tr_done, TRNO["mix", t] + 1)
                            sp.dma_start(resid[:, t, :], xd[t]).then_inc(x_back[t], 16)
                if p == 4 * CNO[("o", 0)] + 3:
                    sp.wait_ge(resid_ready, TT)
                    sp.dma_start(gain[:, :], norm_x_post[0:1, :].broadcast_to([P, D])).then_inc(gains_landed, 16)

            def dn_load(i):
                sp.dma_start(raw[:, dn_slot, :], w_down[bass.ds(i * P, P), :]).then_inc(dn_landed, 16)

            dn_slot, gu_slot = (NPIECE + 4) % NRAW, (NPIECE + 2) % NRAW
            sp.wait_ge(lo_split, ffn_splits(dn_piece(0) - 3))
            dn_load(0)
            sp.wait_ge(resid_ready, 2 * TT)
            sp.dma_start(gain[:, :], norm_ffn_post[0:1, :].broadcast_to([P, D])).then_inc(gains_landed, 16)
            with sp.Fori(2, FT) as i:
                for h in range(2):
                    sp.wait_ge(lo_split, ffn_splits(gu_piece(i, h) - 3))
                    gu_dma(i, h, gu_slot + h, gu_landed[h])
                sp.wait_ge(lo_split, ffn_splits(dn_piece(i - 1) - 3))
                dn_load(i - 1)
            sp.wait_ge(lo_split, ffn_splits(dn_piece(FT - 2)))
            dn_load(FT - 1)
            od = out[0].rearrange("(t p) d -> t p d", p=P)
            for t in range(TT):
                sp.wait_ge(final_ready, t + 1)
                sp.dma_start(od[t], resid[:, t, :]).then_inc(out_stored, 16)
            sp.wait_ge(out_stored, 16 * TT)

        @block.gpsimd
        def _(pool):
            own = [0]

            def link(ins):
                own[0] += 1
                ins.then_inc(pool_own, 1)
                pool.wait_ge(pool_own, own[0])

            pool.memset(ident[:, :], 0.0).then_inc(pool_own, 1)
            pool.memset(later[:, :], 1.0).then_inc(pool_own, 1)
            pool.memset(inchunk[:, :], 0.0).then_inc(pool_own, 1)
            pool.memset(mhalf[:, :], -0.5).then_inc(pool_own, 1)
            pool.memset(wg[:, :], 0.0).then_inc(pool_own, 1)
            own[0] = 5
            pool.wait_ge(pool_own, 5)
            pool.affine_select(out=ident[:, :], in_=ident[:, :], compare_op=ALU.not_equal, fill=1.0,
                               base=0, pattern=[[-1, P]], channel_multiplier=1).then_inc(consts, 1)
            link(pool.affine_select(out=later[:, :], in_=later[:, :], compare_op=ALU.is_gt, fill=0.0,
                                    base=0, pattern=[[-1, P]], channel_multiplier=1))
            pool.memset(later[CHUNK:P, 0:CHUNK], 0.0).then_inc(consts, 1)
            pool.memset(inchunk[0:CHUNK, 0:1], 1.0).then_inc(consts, 1)
            pool.memset(inchunk[CHUNK:P, 1:2], 1.0).then_inc(consts, 1)
            pool.wait_ge(consts, 4)
            for r, src in ((0, w_gate_up[0]), (32, w_gate_up[0]), (CHUNK, b_gate[0:1, :])):
                pool.dma_start(wg[r:r + src.shape[0], :], src).then_inc(small_landed, 16)

            def rstd_of(job):
                kind, t = job
                if kind == "ln":
                    pool.wait_ge(bn_ready, t + 1)
                    v, n = mv[:, t % 2, 1:2], 1
                    link(pool.tensor_scalar(var[:, 0:1], v, EPS, None, ALU.add))
                else:
                    pool.wait_ge(squared, squares(job))
                    s = squares(job) - 1
                    if kind == "gla":
                        n = 4
                        link(pool.tensor_scalar(var[:, 0:4], ss[:, s % 2, 0:4], EPS, None, ALU.add))
                    else:
                        n = 1
                        other = ssh[:, t:t + 1] if kind in ("wo_y", "o_y") else ss[:, s % 2, 1:2]
                        link(pool.tensor_scalar(var[:, 0:1], ss[:, s % 2, 0:1], other, EPS,
                                                ALU.add, ALU.add))
                j = JNO[job]
                ins = pool.tensor_tensor(out=rstd[:, j % 4, 0:n], in0=var[:, 0:n], in1=mhalf[:, 0:n], op=ALU.pow)
                ins.then_inc(rstd_ready, 1)
                pool.wait_ge(rstd_ready, j + 1)

            def store(n):
                o, r = divmod(n, 16)
                b, r = divmod(r, 8)
                pool.wait_ge(free_act, free_count(SNO["xo" if o else "xq", b, r], "act"))
                pool.dma_start((o_dram if o else s_dram)[r * P:(r + 1) * P, b * CW:(b + 1) * CW], stage[:, n % 3, :]).then_inc(stored[n % 3], 16)

            rstd_of(("mem", 0))
            rstd_of(("mem", 1))
            at_step = {SNO["xo" if n >= 16 else "xq", n % 16 // 8, n % 8]: n for n in range(32)}
            for n in range(len(STEPS)):
                if n in X_NORM:
                    rstd_of(("x", X_NORM[n]))
                if n in at_step:
                    store(at_step[n])
            for s in range(3):
                pool.wait_ge(stored[s], 16 * sum((k % 3) == s for k in range(32)))
            pool.memset(wa[:, :, :].bitcast(F32), 0.0).then_inc(consts, 1)
            pool.wait_ge(consts, 5)
            pool.wait_ge(tr_done, TRNO["x", 7] + 1)
            pool.memset(aT[CHUNK:CHUNK + 1, :], 1.0).then_inc(consts, 1)
            pool.wait_ge(consts, 6)
            pool.memset(state[:, 1, 1, :, :], 0.0).then_inc(consts, 1)
            pool.wait_ge(consts, 7)
            for job in JOBS[10:JNO["ffn_y", 0]]:
                rstd_of(job)
            pool.wait_ge(resid_ready, 2 * TT)
            pool.wait_ge(tr_done, len(TRS))
            pool.wait_ge(mm_done, len(STEPS))
            for t in range(TT):
                pool.memset(acc[t], 0.0).then_inc(added, 1)
            for t in range(TT):
                pool.wait_ge(added, TT * (FT - 1) + t + 1)
                if t == 0:
                    pool.wait_ge(gains_landed, 16 * 5)
                pool.wait_ge(squared, squares(("ffn_y", t)))
                rstd_of(("ffn_y", t))
                pool.tensor_tensor(out=acc[t], in0=acc[t], in1=gain[:, :], op=ALU.mult).then_inc(gained, 1)

        @block.scalar
        def _(act):
            own = [0]

            def link(ins):
                own[0] += 1
                ins.then_inc(act_own, 1)
                act.wait_ge(act_own, own[0])

            o = 0
            for _, v, w in VECTORS:
                src = v[0] if len(v.shape) == 3 else v.rearrange("o (k p) -> (o k) p", p=P)
                act.dma_start(wsT[o:o + w, 0, :], src).then_inc(rows_landed, 16)
                o += w
            JUNK = ps[:, Z, :]

            def square(job, parts, after=None):
                s = squares(job) - 1
                if s >= 2:
                    prev = [j for j in JOBS if j[0] != "ln"][s - 2]
                    act.wait_ge(rstd_ready, JNO[prev] + 1)
                sc = DV ** -0.5 if len(parts) == 4 else D ** -0.5
                for i, p_ in enumerate(parts):
                    w = p_.shape[-1]
                    ins = nc.scalar.activation(JUNK[:, 0:w], p_, ACT.Square, scale=sc,
                                               accum_out=ss[:, s % 2, i:i + 1])
                    if i < len(parts) - 1:
                        link(ins)
                ins.then_inc(squared, 1)
                act.wait_ge(squared, s + 1)

            def in_square(g):
                kind, t = g
                if kind == "mem":
                    act.wait_ge(mem_landed, 16)
                else:
                    act.wait_ge(x_landed[t % 2], 16 * (t // 2 + 1))
                square(g, [tok[:, t % 2, 0:CW], tok[:, t % 2, CW:D]])

            def tr_evac(g):
                n = TRNO[g]
                act.wait_ge(tr_done, n + 1)
                if g[0] == "ws":
                    nc.scalar.activation(wsT[:, :, :].rearrange("p a b -> p (a b)"), ps[:, TR, :],
                                         ACT.Copy).then_inc(tr_hi, 2)
                    return
                if g[0] == "xq" and g[1] >= 4:
                    act.wait_ge(mm_done, LAST[1] + 1)
                for b in range(2):
                    nc.scalar.activation(tr_target(g, b, True), tr_bank(g, b), ACT.Copy).then_inc(tr_hi, 1)

            def split(p):
                if p == 0:
                    act.wait_ge(columns_ready, 1)
                landed(act, p)
                slot_free(act, p)
                splits_hi(act, split_parts(p))

            def evac(n):
                kind, b, t = STEPS[n]
                if kind in ("xk", "xv"):
                    act.wait_ge(mm_done, n + 1)
                    f = 4 * b + t + (KT if kind == "xv" else 0)
                    nc.scalar.activation(kv_hi[:, f, :], bank(n, NM), ACT.Copy).then_inc(kv_hi_done, 1)
                elif kind in ("xq", "xo"):
                    act.wait_ge(mm_done, n + 1)
                    m = 8 * b + t + (16 if kind == "xo" else 0)
                    if m >= 3:
                        act.wait_ge(stored[m % 3], 16 * (m // 3))
                    nc.scalar.activation(stage[:, m % 3, :], bank(n), ACT.Copy).then_inc(free_act, 1)
                elif kind == "k":
                    act.wait_ge(mm_done, n + 1)
                    nc.scalar.activation(resid[:, t, CW:CW + KW], bank(n, KW), ACT.Copy).then_inc(free_act, 1)
                    act.wait_ge(z_read, t + 1)
                    zt = resid[:, t, 0:KW]
                    nc.scalar.activation(zt, zt, ACT.Exp).then_inc(gate_e, 1)
                    act.wait_ge(gate_e, t + 1)
                    nc.scalar.activation(zt, zt, ACT.Ln, bias=1.0).then_inc(gate_l, 1)
                elif kind == "v":
                    act.wait_ge(suf_done, t + 1)
                    nc.scalar.activation(resid[:, t, KW:2 * KW], ps[:, SUF, 0:KW], ACT.Exp,
                                         scale=1.0 / GATE_TAU).then_inc(act_own, 1)
                    nc.scalar.activation(decay[:, t, :], ps[:, SUF, KW:KW + 4], ACT.Exp,
                                         scale=1.0 / GATE_TAU).then_inc(suf_read, 1)
                    own[0] += 1
                    act.wait_ge(mm_done, n + 1)
                    nc.scalar.activation(half[:, t, :], bank(n), ACT.Copy).then_inc(free_act, 1)
                elif kind == "g":
                    act.wait_ge(mm_done, n + 1)
                    act.wait_ge(kdec_ready, t + 1)
                    nc.scalar.activation(resid[:, t, 0:GW], bank(n), ACT.Silu).then_inc(free_act, 1)
                    act.wait_ge(o_done, t + 1)
                    square(("gla", t), [o_psum(slice(0, P), h) for h in range(HEADS)])
                elif kind == "sv":
                    act.wait_ge(mm_done, n + 1)
                    if t == 0:
                        act.wait_ge(u_done, TT)
                    nc.scalar.activation(half[:, t, :], bank(n), ACT.Gelu_apprx_tanh).then_inc(free_act, 1)
                elif kind == "u":
                    act.wait_ge(mm_done, n + 1)
                    nc.scalar.activation(resid[:, t, GW:D], bank(n), ACT.Gelu_apprx_tanh).then_inc(free_act, 1)
                elif kind in ("wo", "o"):
                    act.wait_ge(mm_done, n + 1)
                    if b == 0:
                        m = y_first(kind, t)
                        nc.scalar.activation(JUNK, bank(n), ACT.Square, scale=D ** -0.5,
                                             accum_out=ssh[:, t:t + 1]).then_inc(y_squared, 1)
                        act.wait_ge(y_squared, m)
                    else:
                        square((kind + "_y", t), [bank(n)])

                        def new_tile():
                            act.wait_ge(resid_ready, t + 1 + (TT if kind == "o" else 0))
                            square((kind + "_x", t), [resid[:, t, 0:CW], resid[:, t, CW:D]])
                        return new_tile
                elif kind == "s":
                    act.wait_ge(top_ready, 8 * b + t + 1)
                    dst = half[:, t, :] if b == 0 else tok[:, t % 2, 0:CW]
                    if b == 1 and t >= 2:
                        act.wait_ge(tr_done, TRNO["probs", t - 2] + 1)
                    for h in range(2):
                        ins = nc.scalar.activation(dst[:, h * NM:(h + 1) * NM], bank(n)[:, h * NM:(h + 1) * NM],
                                                   ACT.Exp, bias=top[:, t % 2, h:h + 1], scale=XD ** -0.5,
                                                   accum_out=den[:, t % 2, h:h + 1])
                        if h:
                            ins.then_inc(free_act, 1)
                        else:
                            ins.then_inc(exp_ready, 1)

            in_square(("mem", 0))
            in_square(("mem", 1))
            for p in SPLIT_AT[-1]:
                split(p)
            for n in range(len(STEPS) + 1):
                if n < len(STEPS):
                    for g in TR_AT[n]:
                        tr_evac(g)
                if n and STEPS[n - 1] == ("a", 0, 1):
                    nc.scalar.preload_act_table_set("natural_log_exp_and_others")
                more = evac(n - 1) if n else None
                if n < len(STEPS):
                    for p in SPLIT_AT[n]:
                        split(p)
                    if n in X_NORM:
                        in_square(("x", X_NORM[n]))
                if more:
                    more()

            def hidden_act(i, i2, h):
                act.wait_ge(gu_done, i * 2 + (h + 1))
                ph = ps[:, 2 * h, :]
                if not (isinstance(i, int) and i == 0):
                    act.wait_ge(hid_lo, (i - 1) * 2 + (h + 1))
                nc.scalar.activation(hid[h][:, :], ph, ACT.Silu).then_inc(silu_done, 1)
                act.wait_ge(prod_done, i * 2 + (h + 1))
                nc.scalar.activation(hidden(wf_hi, i2)[:, h * CW:(h + 1) * CW], hid[h][:, :],
                                     ACT.Copy).then_inc(hid_hi, 1)

            def gu_split(i, i2, h):
                act.wait_ge(gu_landed[h], i * 32)
                splits_hi(act, gu_parts(i2, h, (NPIECE + 2 + h) % NRAW))

            def dn_split(i, last=False):
                slot = (NPIECE + 4) % NRAW
                act.wait_ge(dn_landed, i * 16 + 16)
                nc.scalar.activation(dn(wf_hi, last), raw[:, slot, :], ACT.Copy).then_inc(hi_split, 1)

            for g in TRS[-LAG:]:
                tr_evac(g)
            for h in range(2):
                hidden_act(0, 0, h)
            with act.Fori(0, (FT - 2) // 2) as jj:
                for e in (1, 2):
                    i = jj * 2 + e
                    act.wait_ge(gu_done, i * 2)
                    dn_split(i - 1)
                    for h in range(2):
                        gu_split(i + 1, (e + 1) % 2, h)
                        hidden_act(i, e % 2, h)
            act.wait_ge(gu_done, (FT - 1) * 2)
            dn_split(FT - 2)
            dn_split(FT - 1, last=True)
            for h in range(2):
                hidden_act(FT - 1, (FT - 1) % 2, h)
            for t in range(TT):
                act.wait_ge(added, TT * (FT - 1) + t + 1)
                square(("ffn_y", t), [acc[t][:, 0:CW], acc[t][:, CW:D]])

        @block.vector
        def _(dve):
            own = [0]

            def link(ins):
                own[0] += 1
                ins.then_inc(dve_own, 1)
                dve.wait_ge(dve_own, own[0])

            def xh(g):
                kind, t = g
                job = {"mem": ("mem", t), "x": ("x", t), "xn2": ("wo_x", t), "xn3": ("o_x", t)}[kind]
                dve.wait_ge(rstd_ready, JNO[job] + 1)
                r = rstd[:, JNO[job] % 4, 0:1]
                if kind in ("mem", "x"):
                    src = tok[:, t % 2, :]
                else:
                    src = resid[:, t, :]
                    if t >= 2:
                        dve.wait_ge(tr_done, TRNO[kind, t - 2] + 1)
                    elif kind == "xn3":
                        dve.wait_ge(tr_done, TRNO["probs", TT - 2 + t] + 1)
                nc.vector.tensor_scalar(tok[:, t % 2, :], src, r, None, ALU.mult).then_inc(xh_ready, 1)

            def tr_evac(g):
                n = TRNO[g]
                if g[0] == "ws":
                    dve.wait_ge(tr_hi, 2 * n + 2)
                    nc.vector.memset(wsT[CHUNK:P, :, 0:CHUNK], 0.0).then_inc(tr_lo, 2)
                    return
                for b in range(2):
                    dve.wait_ge(tr_hi, 2 * n + b + 1)
                    nc.vector.tensor_tensor(tr_target(g, b, False), tr_bank(g, b),
                                            tr_target(g, b, True).bitcast(F32), ALU.subtract).then_inc(tr_lo, 1)

            def split(p):
                dve.wait_ge(hi_split, splits(p) if p < NPIECE else ffn_splits(p))
                splits_lo(dve, split_parts(p))

            def residual(kind, t):
                job = (kind + "_y", t)
                dve.wait_ge(rstd_ready, JNO[job] + 1)
                r = rstd[:, JNO[job] % 4, 0:1]
                if kind == "wo":
                    dve.wait_ge(x_back[t], 16)
                for h, src in enumerate((half[:, t, :], spare[:, :])):
                    ins = nc.vector.scalar_tensor_tensor(
                        out=resid[:, t, h * CW:(h + 1) * CW], in0=src, scalar=r,
                        in1=resid[:, t, h * CW:(h + 1) * CW], op0=ALU.mult, op1=ALU.add)
                    if h == 0:
                        ins.then_inc(dve_own, 1)
                        own[0] += 1
                ins.then_inc(resid_ready, 1)
                dve.wait_ge(resid_ready, t + 1 + (TT if kind == "o" else 0))

            def evac(n):
                kind, b, t = STEPS[n]
                if kind in ("xk", "xv"):
                    f = 4 * b + t + (KT if kind == "xv" else 0)
                    dve.wait_ge(kv_hi_done, f + 1 if kind == "xk" else f + 1)
                    nc.vector.tensor_tensor(kv_lo[:, f, :], bank(n, NM), kv_hi[:, f, :].bitcast(F32),
                                            ALU.subtract).then_inc(free_dve, 1)
                elif kind == "q":
                    pair, hf = divmod(t, 2)
                    dve.wait_ge(mm_done, n + 1)
                    o = CW + KW + pair * P
                    nc.vector.tensor_scalar(resid[:, 4 * hf:4 * hf + 4, o:o + P],
                                            bank(n).rearrange("p (t n) -> p t n", t=4), DK ** -0.5, None,
                                            ALU.mult).then_inc(free_dve, 1)
                elif kind == "a":
                    dve.wait_ge(mm_done, n + 1)
                    nc.vector.tensor_copy(aT[0:CHUNK, t * CW:(t + 1) * CW], bank(n)[0:CHUNK, :]).then_inc(free_dve, 1)
                elif kind == "k":
                    dve.wait_ge(z_done, t + 1)
                    zm, za = resid[:, t, KW:2 * KW], resid[:, t, 0:KW]
                    link(nc.vector.tensor_scalar(zm, ps[:, Z, 0:KW], 0.0, None, ALU.min))
                    nc.vector.scalar_tensor_tensor(out=za, in0=zm, scalar=2.0, in1=ps[:, Z, 0:KW],
                                                   op0=ALU.mult, op1=ALU.subtract).then_inc(z_read, 1)
                    dve.wait_ge(gate_l, t + 1)
                    nc.vector.tensor_tensor(resid[:, t, 0:KW], resid[:, t, KW:2 * KW], resid[:, t, 0:KW],
                                            ALU.subtract).then_inc(loga_ready, 1)
                elif kind == "v":
                    dve.wait_ge(suf_read, t + 1)
                    dve.wait_ge(free_act, free_count(SNO["k", 0, t], "act"))
                    kk = resid[:, t, CW:CW + KW]
                    nc.vector.tensor_tensor(kk, kk, resid[:, t, KW:2 * KW], ALU.mult).then_inc(kdec_ready, 1)
                elif kind == "g":
                    dve.wait_ge(rstd_ready, JNO["gla", t] + 1)
                    r = rstd[:, JNO["gla", t] % 4, :]
                    for h in range(HEADS):
                        hs = slice(h * DV, (h + 1) * DV)
                        ins = nc.vector.scalar_tensor_tensor(out=resid[:, t, hs], in0=o_psum(slice(0, P), h),
                                                             scalar=r[:, h:h + 1], in1=resid[:, t, hs],
                                                             op0=ALU.mult, op1=ALU.mult)
                        if h < HEADS - 1:
                            ins.then_inc(dve_own, 1)
                            own[0] += 1
                    ins.then_inc(gla_ready, 1)
                elif kind == "sv":
                    dve.wait_ge(free_act, free_count(n, "act"))
                    hv = half[:, t, :]
                    link(nc.vector.bn_stats(bn[:, :], hv))
                    nc.vector.bn_aggr(mv[:, t % 2, :], bn[:, :]).then_inc(bn_ready, 1)
                    dve.wait_ge(bn_ready, t + 1)
                    dve.wait_ge(rstd_ready, JNO["ln", t] + 1)
                    link(nc.vector.tensor_scalar(hv, hv, mv[:, t % 2, 0:1], rstd[:, JNO["ln", t] % 4, 0:1],
                                                 ALU.subtract, ALU.mult))
                    dve.wait_ge(gains_landed, 32)
                    link(nc.vector.tensor_tensor(hv, hv, gain[:, 0:GW], ALU.mult))
                    nc.vector.tensor_tensor(hv, hv, gain[:, GW:D], ALU.add).then_inc(ln_ready, 1)
                elif kind == "u":
                    dve.wait_ge(free_act, free_count(n, "act"))
                    dve.wait_ge(sg_done, t + 1)
                    for h in range(HEADS):
                        us = resid[:, t, GW + h * P:GW + (h + 1) * P]
                        ins = nc.vector.scalar_tensor_tensor(out=us, in0=sg_psum(t, h),
                                                             scalar=bsp[:, h:h + 1], in1=us,
                                                             op0=ALU.add, op1=ALU.mult)
                        if h < HEADS - 1:
                            ins.then_inc(dve_own, 1)
                            own[0] += 1
                    ins.then_inc(mix_ready, 1)
                elif kind in ("wo", "o"):
                    if b == 0:
                        dve.wait_ge(y_squared, y_first(kind, t))
                    else:
                        dve.wait_ge(squared, squares((kind + "_y", t)))
                    if t == 0 and b == 0:
                        dve.wait_ge(gains_landed, 48 if kind == "wo" else 64)
                    if kind == "o" and b == 0:
                        dve.wait_ge(tr_done, TRNO["probs", t] + 1)
                    if b == 0:
                        nc.vector.tensor_tensor(half[:, t, :], bank(n), gain[:, 0:CW], ALU.mult).then_inc(free_dve, 1)
                    else:
                        nc.vector.tensor_tensor(spare[:, :], bank(n), gain[:, CW:D], ALU.mult).then_inc(free_dve, 1)
                        dve.wait_ge(free_dve, free_count(n, "dve"))
                        return lambda: residual(kind, t)
                elif kind == "s":
                    dve.wait_ge(mm_done, n + 1)
                    if 8 * b + t >= 2:
                        dve.wait_ge(free_act, free_count(n - 2, "act"))
                    link(nc.vector.tensor_reduce(top[:, t % 2, :], bank(n).rearrange("p (h m) -> p h m", h=2),
                                                 AX.X, ALU.max))
                    nc.vector.tensor_scalar(top[:, t % 2, :], top[:, t % 2, :], -(XD ** -0.5), None,
                                            ALU.mult).then_inc(top_ready, 1)

                    def probs():
                        dve.wait_ge(free_act, free_count(n, "act"))
                        link(nc.vector.reciprocal(den[:, t % 2, :], den[:, t % 2, :]))
                        dst = half[:, t, :] if b == 0 else tok[:, t % 2, 0:CW]
                        for h in range(2):
                            v = dst[:, h * NM:(h + 1) * NM]
                            ins = nc.vector.tensor_scalar(v, v, den[:, t % 2, h:h + 1], None, ALU.mult)
                            if h == 0:
                                ins.then_inc(dve_own, 1)
                                own[0] += 1
                        ins.then_inc(probs_ready, 1)
                        dve.wait_ge(probs_ready, 8 * b + t + 1)
                    return probs
                return None

            def scan(t):
                dve.wait_ge(u_done, t + 1)
                if t == 0:
                    dve.wait_ge(consts, 7)
                if t >= 2:
                    dve.wait_ge(o_done, t - 1)
                if t:
                    dve.wait_ge(state_ready, t)
                for c in range(2):
                    for pr in range(2):
                        prev = state[:, (t + 1) % 2, 1, pr, :] if c == 0 else state[:, t % 2, 0, pr, :]
                        ins = nc.vector.scalar_tensor_tensor(
                            out=state[:, t % 2, c, pr, :], in0=prev, scalar=decay[:, t, 2 * pr + c:2 * pr + c + 1],
                            in1=kv_psum(slice(0, P), c, pr), op0=ALU.mult, op1=ALU.add)
                        if (c, pr) != (1, 1):
                            link(ins)
                ins.then_inc(state_ready, 1)

            dve.wait_ge(rows_turned, 1)
            nc.vector.tensor_copy(columns[:, :], ps[:, O, 0:NVEC]).then_inc(columns_ready, 1)
            dve.wait_ge(columns_ready, 1)
            xh(("mem", 0))
            xh(("mem", 1))
            for p in SPLIT_AT[-1]:
                split(p)
            for n in range(len(STEPS) + 2):
                if n < len(STEPS):
                    for g in TR_AT[n]:
                        tr_evac(g)
                if n >= 2:
                    kind, b, t = STEPS[n - 2]
                    if kind in ("wo", "o") and b == 1:
                        xh(("xn2" if kind == "wo" else "xn3", t))
                then = None
                if n and n <= len(STEPS):
                    then = evac(n - 1)
                if n < len(STEPS):
                    for p in SPLIT_AT[n]:
                        split(p)
                    if STEPS[n][:2] == ("g", 0):
                        scan(STEPS[n][2])
                    if n in X_NORM:
                        xh(("x", X_NORM[n]))
                    if STEPS[n] == ("xo", 1, 7):
                        dve.wait_ge(part_landed, 32)
                        dve.wait_ge(small_landed, 16 * 3)
                        dve.wait_ge(consts, 5)
                        for k in range(KT):
                            ins = nc.vector.tensor_scalar(raw_a[:, k, :], raw_a[:, k, :], pre["mix"][:, k:k + 1],
                                                          None, ALU.mult)
                            ins.then_inc(dve_own, 1)
                        own[0] += KT
                        dve.wait_ge(dve_own, own[0])
                        link(nc.vector.tensor_copy(wa[:, :, 0:RANK], raw_a[:, :, :]))
                        nc.vector.tensor_tensor(wa[:, :, 32:32 + RANK], raw_a[:, :, :],
                                                wa[:, :, 0:RANK].bitcast(F32), ALU.subtract).then_inc(wa_ready, 1)
                if then:
                    then()

            def hidden_lo(i, i2, h):
                dve.wait_ge(silu_done, i * 2 + (h + 1))
                nc.vector.tensor_tensor(hid[h][:, :], hid[h][:, :], ps[:, 2 * h + 1, :],
                                        ALU.mult).then_inc(prod_done, 1)
                dve.wait_ge(hid_hi, i * 2 + (h + 1))
                hs = slice(h * CW, (h + 1) * CW)
                nc.vector.tensor_tensor(hidden(wf_lo, i2)[:, hs], hid[h][:, :],
                                        hidden(wf_hi, i2)[:, hs].bitcast(F32), ALU.subtract).then_inc(hid_lo, 1)

            def gu_split(i, i2, h):
                dve.wait_ge(hi_split, ffn_splits(gu_piece(i, h)))
                splits_lo(dve, gu_parts(i2, h, (NPIECE + 2 + h) % NRAW))

            def dn_split(i, last=False):
                dve.wait_ge(hi_split, ffn_splits(dn_piece(i)))
                nc.vector.tensor_tensor(dn(wf_lo, last), raw[:, (NPIECE + 4) % NRAW, :],
                                        dn(wf_hi, last).bitcast(F32), ALU.subtract).then_inc(lo_split, 1)

            def add_down(count, tiles):
                for t in tiles:
                    dve.wait_ge(dn_done, count + (t + 1))
                    o = 4 + 2 * (t % 2)
                    a3 = acc[t].rearrange("p (a n) -> p a n", a=2)
                    nc.vector.tensor_tensor(a3, ps[:, o:o + 2, :], a3, ALU.add).then_inc(added, 1)

            for g in TRS[-LAG:]:
                tr_evac(g)
            for h in range(2):
                hidden_lo(0, 0, h)
            with dve.Fori(0, (FT - 2) // 2) as jj:
                for e in (1, 2):
                    i = jj * 2 + e
                    dn_split(i - 1)
                    gu_split(i + 1, (e + 1) % 2, 0)
                    dve.wait_ge(added, i * TT)
                    add_down((i - 1) * TT, (0, 1))
                    hidden_lo(i, e % 2, 0)
                    add_down((i - 1) * TT, (2, 3))
                    gu_split(i + 1, (e + 1) % 2, 1)
                    add_down((i - 1) * TT, (4, 5, 6, 7))
                    hidden_lo(i, e % 2, 1)
            dn_split(FT - 2)
            dn_split(FT - 1, last=True)
            for h in range(2):
                hidden_lo(FT - 1, (FT - 1) % 2, h)
            dve.wait_ge(added, (FT - 1) * TT)

            def final(t):
                dve.wait_ge(gained, t + 1)
                dve.wait_ge(rstd_ready, JNO["ffn_y", t] + 1)
                nc.vector.scalar_tensor_tensor(out=resid[:, t, :], in0=acc[t],
                                               scalar=rstd[:, JNO["ffn_y", t] % 4, 0:1], in1=resid[:, t, :],
                                               op0=ALU.mult, op1=ALU.add).then_inc(final_ready, 1)

            for t in range(TT + 2):
                if t < TT:
                    dve.wait_ge(dn_done, TT * (FT - 2) + t + 1)
                    o = 4 + 2 * (t % 2)
                    a3 = acc[t].rearrange("p (a n) -> p a n", a=2)
                    nc.vector.tensor_tensor(a3, ps[:, o:o + 2, :], a3, ALU.add).then_inc(added, 1)
                if t >= 2:
                    final(t - 2)

        @block.tensor
        def _(pe):
            def three(out_, lhs, rhs, first, last):
                (lh, ll), (rh, rl) = lhs, rhs
                nc.tensor.matmul(out_, lh, rh, start=first, stop=False)
                nc.tensor.matmul(out_, lh, rl, start=False, stop=False)
                return nc.tensor.matmul(out_, ll, rh, start=False, stop=last)

            def transposes(g):
                kind, i = g
                n = TRNO[g]
                if n:
                    pe.wait_ge(tr_lo, 2 * n)
                if kind in ("mem", "x", "xn2", "xn3"):
                    pe.wait_ge(xh_ready, XHNO[kind, i] + 1)
                elif kind == "xq":
                    p = 4 * (1 + 2 * (i // 4)) + i % 4
                    landed(pe, p)
                elif kind == "mix":
                    pe.wait_ge(mix_ready, i + 1)
                    pe.wait_ge(gla_ready, i + 1)
                elif kind == "probs":
                    pe.wait_ge(probs_ready, TT + i + 1)
                elif kind == "ws":
                    pe.wait_ge(part_landed, 32)
                for j, s in enumerate(tr_source(g)):
                    ins = nc.tensor.transpose(ps[:, TR + j // 4, (j % 4) * P:(j % 4 + 1) * P], s, ident[:, :])
                ins.then_inc(tr_done, 1)

            def linear(n, t, w=CW, off=0):
                c = chunk_of(STEPS[n])
                s = c % 2
                for k in range(KT):
                    if n == FIRST[c] and k % 2 == 0:
                        pe.wait_ge(lo_split, splits(4 * c + k // 2))
                    ks = slice(t * P, (t + 1) * P)
                    ins = three(bank(n, w), (act_hi[:, k, ks], act_lo[:, k, ks]),
                                (w_hi[:, s, k, off:off + w], w_lo[:, s, k, off:off + w]), k == 0, k == KT - 1)
                ins.then_inc(mm_done, 1)

            pe.wait_ge(consts, 1)
            pe.wait_ge(rows_landed, 16 * len(VECTORS))
            nc.tensor.transpose(ps[:, O, 0:NVEC], vec_rows, ident[0:NVEC, 0:NVEC]).then_inc(rows_turned, 1)
            for n, (kind, b, t) in enumerate(STEPS):
                c = chunk_of(STEPS[n])
                s = c % 2
                for g in TR_AT[n]:
                    transposes(g)
                if kind == "k":
                    if t == 0:
                        pe.wait_ge(small_landed, 16 * 3)
                        pe.wait_ge(free_dve, free_count(SNO["a", 0, 1], "dve"))
                        pe.wait_ge(consts, 7)
                    else:
                        pe.wait_ge(z_read, t)
                    nc.tensor.matmul(ps[:, Z, 0:KW], aT[0:CHUNK + 1, t * P:(t + 1) * P], wg[0:CHUNK + 1, :],
                                     start=True, stop=True).then_inc(z_done, 1)
                if kind == "v":
                    pe.wait_ge(loga_ready, t + 1)
                    if t:
                        pe.wait_ge(suf_read, t)
                    lg = resid[:, t, 0:KW]
                    nc.tensor.matmul(ps[:, SUF, 0:KW], later[:, :], lg, start=True, stop=True)
                    for pr in range(2):
                        ins = nc.tensor.matmul(ps[:, SUF, KW + 2 * pr:KW + 2 * pr + 2],
                                               resid[:, t, pr * P:(pr + 1) * P], inchunk[:, :], start=True, stop=True)
                    ins.then_inc(suf_done, 1)
                if kind == "g" or (kind, t) == ("sv", 0):
                    if kind == "sv" or t:
                        o = t - 1 if kind == "g" else TT - 1
                        pe.wait_ge(state_ready, o + 1)
                        if o:
                            pe.wait_ge(gla_ready, o)
                        for cc in range(2):
                            for h in range(HEADS):
                                hp = slice(DK * (h % 2), DK * (h % 2) + DK)
                                cs = CW + KW + P * (h // 2) + CHUNK * cc
                                ins = nc.tensor.matmul(o_psum(slice(CHUNK * cc, CHUNK * (cc + 1)), h),
                                                       resid[hp, o, cs:cs + CHUNK],
                                                       state[hp, o % 2, cc, h // 2, :], start=True, stop=True)
                        ins.then_inc(o_done, 1)
                if kind == "g":
                    pe.wait_ge(kdec_ready, t + 1)
                    pe.wait_ge(free_act, free_count(SNO["v", 0, t], "act"))
                    if t:
                        pe.wait_ge(state_ready, t)
                    for cc in range(2):
                        cp = slice(CHUNK * cc, CHUNK * (cc + 1))
                        for h in range(HEADS):
                            hp = slice(DK * (h % 2), DK * (h % 2) + DK)
                            ins = nc.tensor.matmul(kv_psum(hp, cc, h // 2),
                                                   resid[cp, t, CW + h * DK:CW + (h + 1) * DK],
                                                   half[cp, t, h * DV:(h + 1) * DV], start=True, stop=True)
                    ins.then_inc(u_done, 1)
                if kind == "u":
                    pe.wait_ge(ln_ready, t + 1)
                    if t == 0:
                        pe.wait_ge(gla_ready, TT)
                    elif t >= 2:
                        pe.wait_ge(mix_ready, t - 1)
                    for h in range(HEADS):
                        ins = nc.tensor.matmul(sg_psum(t, h), wsT[:, h, :],
                                               half[:, t, h * P:(h + 1) * P], start=True, stop=True)
                    ins.then_inc(sg_done, 1)

                wait_free(pe, n)
                if kind in ("xk", "xv"):
                    if t == 0 and b == 0 and kind == "xk":
                        pe.wait_ge(tr_lo, 2 * (TRNO["mem", 1] + 1))
                    for k in range(KT):
                        if t == 0 and k % 2 == 0:
                            pe.wait_ge(lo_split, splits(4 * c + k // 2))
                        fs = slice(t * P, (t + 1) * P)
                        ins = three(bank(n, NM), (w_hi[:, s, k, fs], w_lo[:, s, k, fs]),
                                    (memT_hi[:, k, :], memT_lo[:, k, :]), k == 0, k == KT - 1)
                    ins.then_inc(mm_done, 1)
                elif kind == "xq":
                    pe.wait_ge(tr_lo, 2 * (TRNO["xq", 4 * b + t // 2] + 1))
                    if t == 0:
                        pe.wait_ge(free_dve, free_count(SNO["xk", b, 3], "dve"))
                    qv = [w[:, s, :, :].rearrange("p k n -> p (k n)").rearrange("p (f d) -> p f d", f=4)
                          for w in (w_hi, w_lo)]
                    for h in range(2):
                        for f in range(2):
                            fo = 2 * h + f
                            ins = three(bank(n)[:, h * NM:(h + 1) * NM],
                                        tuple(v[:, fo, t * P:(t + 1) * P] for v in qv),
                                        (kv_hi[:, 4 * b + fo, :], kv_lo[:, 4 * b + fo, :]), f == 0, f == 1)
                    ins.then_inc(mm_done, 1)
                elif kind == "xo":
                    h, m = divmod(t, MT)
                    if t == 0 and b == 0:
                        pe.wait_ge(free_dve, free_count(SNO["xv", 1, 3], "dve"))
                    for f in range(2):
                        k = 2 * h + f
                        if t % 2 == 0 and f == 0:
                            pe.wait_ge(lo_split, splits(4 * c + h))
                        ins = three(bank(n), tuple(v[:, KT + k, m * P:(m + 1) * P] for v in (kv_hi, kv_lo)),
                                    (w_hi[:, s, k, :], w_lo[:, s, k, :]), f == 0, f == 1)
                    ins.then_inc(mm_done, 1)
                elif kind == "q":
                    pair, hf = divmod(t, 2)
                    if hf == 0 and pair == 0:
                        pe.wait_ge(tr_lo, 2 * (TRNO["x", 7] + 1))
                    for k in range(KT):
                        if t == 0 and k % 2 == 0:
                            pe.wait_ge(lo_split, splits(4 * c + k // 2))
                        qs, ts = slice(pair * P, (pair + 1) * P), slice(hf * CW, (hf + 1) * CW)
                        ins = three(bank(n), (w_hi[:, s, k, qs], w_lo[:, s, k, qs]),
                                    (act_hi[:, k, ts], act_lo[:, k, ts]), k == 0, k == KT - 1)
                    ins.then_inc(mm_done, 1)
                elif kind == "a":
                    if t == 0:
                        pe.wait_ge(wa_ready, 1)
                    for k in range(KT):
                        ts = slice(t * CW, (t + 1) * CW)
                        nc.tensor.matmul(bank(n)[0:CHUNK, :], wa[:, k, :], act_hi[:, k, ts], start=(k == 0), stop=False)
                        ins = nc.tensor.matmul(bank(n)[0:CHUNK, :], wa[:, k, :], act_lo[:, k, ts],
                                               start=False, stop=(k == KT - 1))
                    ins.then_inc(mm_done, 1)
                elif kind == "k":
                    linear(n, t, KW, KW)
                else:
                    first = {"wo": "mix", "s": "xn2", "o": "probs"}.get(kind)
                    if first and b == 0:
                        pe.wait_ge(tr_lo, 2 * (TRNO[first, t] + 1))
                    linear(n, t)

            def gate_up(i2, h, g, ks=range(KT)):
                for k in ks:
                    ts = slice(h * CW, (h + 1) * CW)
                    ins = three(ps[:, 2 * h + g, :],
                                (gu(wf_hi, i2)[:, k, g, :], gu(wf_lo, i2)[:, k, g, :]),
                                (act_hi[:, k, ts], act_lo[:, k, ts]), k == 0, k == KT - 1)
                if g == 0:
                    ins.then_inc(gu_done, 1)

            def down(i2, t, first=True, last=True, final=False):
                ts = slice(t * P, (t + 1) * P)
                for h in range(2):
                    hs = slice(h * CW, (h + 1) * CW)
                    ins = three(ps[:, 4 + 2 * (t % 2) + h, :],
                                (hidden(wf_hi, i2)[:, ts], hidden(wf_lo, i2)[:, ts]),
                                (dn(wf_hi, final)[:, hs], dn(wf_lo, final)[:, hs]), first, last)
                if last:
                    ins.then_inc(dn_done, 1)

            pe.wait_ge(free_dve, free_count(len(STEPS) - 2, "dve"))
            pe.wait_ge(lo_split, ffn_splits(gu_piece(0, 1)))
            rest = TRS[-LAG:]
            pe.wait_ge(tr_lo, 2 * (TRNO["xn3", 3] + 1))

            gate_up(0, 0, 1)
            transposes(rest[0])
            pe.wait_ge(free_dve, free_count(len(STEPS) - 1, "dve"))
            gate_up(0, 0, 0)
            transposes(rest[1])
            transposes(rest[2])
            pe.wait_ge(tr_lo, 2 * len(TRS))
            pe.wait_ge(squared, squares(("o_x", TT - 1)))
            gate_up(0, 1, 1)
            gate_up(0, 1, 0)
            with pe.Fori(0, (FT - 2) // 2) as jj:
                for e in (1, 2):
                    i = jj * 2 + e

                    def down_pair(t):
                        for tt in (t, t + 1):
                            pe.wait_ge(added, i * TT + (tt - 1))
                            down((e - 1) % 2, tt)

                    pe.wait_ge(lo_split, ffn_splits(gu_piece(i, 1)))
                    pe.wait_ge(prod_done, i * 2 - 1)
                    gate_up(e % 2, 0, 1)
                    pe.wait_ge(lo_split, ffn_splits(dn_piece(i - 1)))
                    pe.wait_ge(hid_lo, i * 2)
                    down_pair(0)
                    gate_up(e % 2, 0, 0)
                    down_pair(2)
                    pe.wait_ge(prod_done, i * 2)
                    gate_up(e % 2, 1, 1, range(KT // 2))
                    down_pair(4)
                    gate_up(e % 2, 1, 1, range(KT // 2, KT))
                    down_pair(6)
                    gate_up(e % 2, 1, 0)
            i = FT - 1
            for h in range(2):
                pe.wait_ge(prod_done, 2 * i + h - 1)
                if h == 0:
                    pe.wait_ge(lo_split, ffn_splits(gu_piece(i, 1)))
                for g in (1, 0):
                    gate_up(i % 2, h, g)
            pe.wait_ge(lo_split, ffn_splits(dn_piece(i)))
            n0 = TT * (FT - 1)
            for t in range(TT):
                if t == 0:
                    for tt in range(2):
                        pe.wait_ge(added, n0 - 1 + tt)
                        down((i - 1) % 2, tt, True, False)
                    pe.wait_ge(hid_lo, 2 * FT)
                elif t >= 2:
                    pe.wait_ge(added, n0 + t - 1)
                    down((i - 1) % 2, t, True, False)
                down(i % 2, t, False, True, final=True)


_INS = ["x", "mem", "norm_mix_pre", "w_in", "w_gate_up", "b_gate", "gla_onorm", "sg_ln_g", "sg_ln_b",
        "w_spatial", "b_spatial", "w_out", "norm_mix_post", "norm_x_pre", "norm_mem", "w_xq", "w_xkv",
        "w_xo", "norm_x_post", "norm_ffn_pre", "w_ffn_gu", "w_ffn_down", "norm_ffn_post"]


def kernel(**inputs):
    import numpy as _np
    import concourse.bacc as _bacc
    from concourse import mybir as _mybir
    from concourse.bass_utils import run_bass_kernel_spmd as _run

    nc = _bacc.Bacc("TRN2", target_bir_lowering=False, num_devices=1)
    arrays, args = {}, []
    for name in _INS:
        a = _np.ascontiguousarray(inputs[name])
        arrays[f"in_{name}"] = a
        args.append(nc.dram_tensor(f"in_{name}", a.shape, _mybir.dt.from_np(a.dtype), kind="ExternalInput").ap())
    shape = inputs["x"].shape
    args.append(nc.dram_tensor("out_y", shape, _mybir.dt.float32, kind="ExternalOutput").ap())
    build(nc, *args)
    r = _run(nc, [arrays], core_ids=[0])
    return r.results[0]["out_y"]
```
